# Optimizing a Trainium2 kernel written in Bass

```python
import math
import jax, jax.numpy as jnp
from jax import lax
import numpy as np

D_MODEL = 1024
BATCH = 1
SEQ = 256
DEPTH = 2

NORM_EPS = 1e-6
D_FF = 2816
FFN_RES_SCALE = 0.5
CONV_K = 4

SSD_HEADS = 16
SSD_HEAD_DIM = 64
SSD_WIDTH = SSD_HEADS * SSD_HEAD_DIM
SSD_GROUPS = 2
SSD_STATE = 128
SSD_CHUNK = 128
SSD_XBC = SSD_WIDTH + 2 * SSD_GROUPS * SSD_STATE

LRU_WIDTH = 1024
LRU_BLOCKS = 16
LRU_BLOCK_DIM = LRU_WIDTH // LRU_BLOCKS
LRU_C = 8.0

HYB_IN = SSD_WIDTH + SSD_XBC + SSD_HEADS + LRU_WIDTH + LRU_WIDTH
HYB_SPLITS = (SSD_WIDTH,
              SSD_WIDTH + SSD_XBC,
              SSD_WIDTH + SSD_XBC + SSD_HEADS,
              SSD_WIDTH + SSD_XBC + SSD_HEADS + LRU_WIDTH)
HYB_OUT = SSD_WIDTH + LRU_WIDTH

DIFF_HEADS = 8
DIFF_HEAD_DIM = 64
DIFF_WIDTH = DIFF_HEADS * 2 * DIFF_HEAD_DIM
Q_BLOCK = 128
ROPE_THETA = 500000.0
ROT_DIM = DIFF_HEAD_DIM // 4

N_EVEN = (DEPTH + 1) // 2
N_ODD = DEPTH // 2

kernel_name = "hybrid_ssd_rglru_diffattn_macaron"

def rms_norm(x, w, eps=NORM_EPS):
    xf = x.astype(jnp.float32)
    y = xf * lax.rsqrt(jnp.mean(xf * xf, axis=-1, keepdims=True) + eps)
    return (y * w.astype(jnp.float32)).astype(x.dtype)

def swiglu(x, w_gate, w_up, w_down):
    return (jax.nn.silu(x @ w_gate) * (x @ w_up)) @ w_down

def causal_dwconv(x, w, b):
    k = w.shape[0]
    y = lax.conv_general_dilated(x, w[:, None, :].astype(x.dtype), window_strides=(1,),
                                 padding=((k - 1, 0),),
                                 dimension_numbers=('NWC', 'WIO', 'NWC'),
                                 feature_group_count=x.shape[-1])
    return y + b

def ssd_chunked(x, dt, a, bmat, cmat):
    bsz, l, h, p = x.shape
    g, n = bmat.shape[-2:]
    r = h // g
    c = l // SSD_CHUNK
    q = SSD_CHUNK
    xs = (x.astype(jnp.float32) * dt[..., None]).reshape(bsz, c, q, g, r, p)
    bc = bmat.astype(jnp.float32).reshape(bsz, c, q, g, n)
    cc = cmat.astype(jnp.float32).reshape(bsz, c, q, g, n)
    cs = jnp.cumsum((dt * a).reshape(bsz, c, q, g, r), axis=2)
    mask = jnp.tril(jnp.ones((q, q), dtype=bool))[:, :, None, None]
    seg = cs[:, :, :, None] - cs[:, :, None, :]
    decay = jnp.exp(jnp.where(mask, seg, -jnp.inf))
    cb = jnp.einsum('bcign,bcjgn->bcijg', cc, bc)
    y_diag = jnp.einsum('bcijg,bcijgr,bcjgrp->bcigrp', cb, decay, xs)
    decay_to_end = jnp.exp(cs[:, :, -1:] - cs)
    states = jnp.einsum('bcjgn,bcjgr,bcjgrp->bcgrpn', bc, decay_to_end, xs)
    chunk_decay = jnp.exp(cs[:, :, -1])

    def step(s, inp):
        st, dec = inp
        return s * dec[..., None, None] + st, s

    s0 = jnp.zeros((bsz, g, r, p, n), jnp.float32)
    _, prev = lax.scan(step, s0, (jnp.swapaxes(states, 0, 1), jnp.swapaxes(chunk_decay, 0, 1)))
    prev = jnp.swapaxes(prev, 0, 1)
    y_off = jnp.einsum('bcign,bcgrpn,bcigr->bcigrp', cc, prev, jnp.exp(cs))
    return (y_diag + y_off).reshape(bsz, l, h, p)

def ssd_mixer(z, xbc, dt_raw, conv_w, conv_b, dt_bias, a_log, d_skip, norm_w):
    bsz, l, _ = xbc.shape
    xbc = jax.nn.silu(causal_dwconv(xbc, conv_w, conv_b))
    xa = xbc[..., :SSD_WIDTH].reshape(bsz, l, SSD_HEADS, SSD_HEAD_DIM)
    bm = xbc[..., SSD_WIDTH:SSD_WIDTH + SSD_GROUPS * SSD_STATE].reshape(bsz, l, SSD_GROUPS, SSD_STATE)
    cm = xbc[..., SSD_WIDTH + SSD_GROUPS * SSD_STATE:].reshape(bsz, l, SSD_GROUPS, SSD_STATE)
    dt = jax.nn.softplus(dt_raw.astype(jnp.float32) + dt_bias.astype(jnp.float32))
    a = -jnp.exp(a_log.astype(jnp.float32))
    y = ssd_chunked(xa, dt, a, bm, cm)
    y = y + d_skip.astype(jnp.float32)[:, None] * xa.astype(jnp.float32)
    y = y.reshape(bsz, l, SSD_WIDTH).astype(z.dtype)
    yg = (y * jax.nn.silu(z)).reshape(bsz, l, SSD_GROUPS, SSD_WIDTH // SSD_GROUPS)
    yg = rms_norm(yg, norm_w.reshape(SSD_GROUPS, SSD_WIDTH // SSD_GROUPS))
    return yg.reshape(bsz, l, SSD_WIDTH)

def rglru_mixer(gate, xb, conv_w, conv_b, w_ra, b_ra, w_ix, b_ix, lam):
    bsz, l, d = xb.shape
    xb = causal_dwconv(xb, conv_w, conv_b)
    xh = xb.reshape(bsz, l, LRU_BLOCKS, LRU_BLOCK_DIM)
    r_t = jax.nn.sigmoid(jnp.einsum('blhi,hij->blhj', xh, w_ra).reshape(bsz, l, d) + b_ra)
    i_t = jax.nn.sigmoid(jnp.einsum('blhi,hij->blhj', xh, w_ix).reshape(bsz, l, d) + b_ix)
    log_a = -LRU_C * r_t.astype(jnp.float32) * jax.nn.softplus(-lam.astype(jnp.float32))
    a_t = jnp.exp(log_a)
    mult = jnp.sqrt(-jnp.expm1(2.0 * log_a))
    u = mult * (i_t * xb).astype(jnp.float32)

    def combine(left, right):
        a1, b1 = left
        a2, b2 = right
        return a1 * a2, a2 * b1 + b2

    _, h = lax.associative_scan(combine, (a_t, u), axis=1)
    return jax.nn.gelu(gate) * h.astype(gate.dtype)

def rope_tables(seq):
    inv = ROPE_THETA ** (-jnp.arange(0, ROT_DIM, 2, dtype=jnp.float32) / ROT_DIM)
    ang = jnp.arange(seq, dtype=jnp.float32)[:, None] * inv[None, :]
    return jnp.cos(ang), jnp.sin(ang)

def apply_partial_rope(t, cos, sin):
    half = ROT_DIM // 2
    c = cos[None, :, None, None, :].astype(t.dtype)
    s = sin[None, :, None, None, :].astype(t.dtype)
    t1, t2, rest = t[..., :half], t[..., half:ROT_DIM], t[..., ROT_DIM:]
    return jnp.concatenate([t1 * c - t2 * s, t2 * c + t1 * s, rest], axis=-1)

def diff_attention(h, w_qkv, lq1, lk1, lq2, lk2, subln_w, w_o, lambda_init, cos, sin):
    bsz, s, _ = h.shape
    q, k, v = jnp.split(h @ w_qkv, 3, axis=-1)
    q = apply_partial_rope(q.reshape(bsz, s, DIFF_HEADS, 2, DIFF_HEAD_DIM), cos, sin) * (DIFF_HEAD_DIM ** -0.5)
    k = apply_partial_rope(k.reshape(bsz, s, DIFF_HEADS, 2, DIFF_HEAD_DIM), cos, sin)
    v = v.reshape(bsz, s, DIFF_HEADS, 2 * DIFF_HEAD_DIM)
    lam = (jnp.exp(jnp.sum(lq1.astype(jnp.float32) * lk1.astype(jnp.float32)))
           - jnp.exp(jnp.sum(lq2.astype(jnp.float32) * lk2.astype(jnp.float32))) + lambda_init)
    outs = []
    for qb in range(s // Q_BLOCK):
        lo = qb * Q_BLOCK
        hi = lo + Q_BLOCK
        scores = jnp.einsum('bqhcd,bkhcd->bhcqk', q[:, lo:hi], k[:, :hi]).astype(jnp.float32)
        mask = (lo + jnp.arange(Q_BLOCK))[:, None] >= jnp.arange(hi)[None, :]
        p = jax.nn.softmax(jnp.where(mask, scores, -jnp.inf), axis=-1)
        attn = p[:, :, 0] - lam * p[:, :, 1]
        outs.append(jnp.einsum('bhqk,bkhe->bqhe', attn.astype(v.dtype), v[:, :hi]))
    o = jnp.concatenate(outs, axis=1)
    o = rms_norm(o, subln_w) * (1.0 - lambda_init)
    return o.reshape(bsz, s, DIFF_WIDTH) @ w_o

def setup_inputs(seed: int = 0) -> dict:
    key = jax.random.key(seed)
    ks = iter(jax.random.split(key, 64))

    def normal(shape, scale):
        return scale * jax.random.normal(next(ks), shape, jnp.float32)

    def gain(shape):
        return 1.0 + normal(shape, 0.02)

    def uniform(shape, lo, hi):
        return jax.random.uniform(next(ks), shape, jnp.float32, lo, hi)

    dt0 = jnp.exp(uniform((N_EVEN, SSD_HEADS), math.log(1e-3), math.log(1e-1)))
    a_pow = uniform((N_EVEN, LRU_WIDTH), 0.9, 0.999)
    a_base = a_pow ** (1.0 / LRU_C)
    return {
        "x": normal((BATCH, SEQ, D_MODEL), 1.0),
        "norm_ff1": gain((DEPTH, D_MODEL)),
        "ffn1_gate": normal((DEPTH, D_MODEL, D_FF), D_MODEL ** -0.5),
        "ffn1_up": normal((DEPTH, D_MODEL, D_FF), D_MODEL ** -0.5),
        "ffn1_down": normal((DEPTH, D_FF, D_MODEL), D_FF ** -0.5),
        "norm_mix": gain((DEPTH, D_MODEL)),
        "norm_ff2": gain((DEPTH, D_MODEL)),
        "ffn2_gate": normal((DEPTH, D_MODEL, D_FF), D_MODEL ** -0.5),
        "ffn2_up": normal((DEPTH, D_MODEL, D_FF), D_MODEL ** -0.5),
        "ffn2_down": normal((DEPTH, D_FF, D_MODEL), D_FF ** -0.5),
        "hyb_w_in": normal((N_EVEN, D_MODEL, HYB_IN), D_MODEL ** -0.5),
        "ssd_conv_w": normal((N_EVEN, CONV_K, SSD_XBC), CONV_K ** -0.5),
        "ssd_conv_b": normal((N_EVEN, SSD_XBC), 0.02),
        "ssd_dt_bias": dt0 + jnp.log(-jnp.expm1(-dt0)),
        "ssd_a_log": jnp.log(uniform((N_EVEN, SSD_HEADS), 1.0, 16.0)),
        "ssd_d": gain((N_EVEN, SSD_HEADS)),
        "ssd_norm": gain((N_EVEN, SSD_WIDTH)),
        "lru_conv_w": normal((N_EVEN, CONV_K, LRU_WIDTH), CONV_K ** -0.5),
        "lru_conv_b": normal((N_EVEN, LRU_WIDTH), 0.02),
        "lru_w_ra": normal((N_EVEN, LRU_BLOCKS, LRU_BLOCK_DIM, LRU_BLOCK_DIM), LRU_BLOCK_DIM ** -0.5),
        "lru_b_ra": normal((N_EVEN, LRU_WIDTH), 0.02),
        "lru_w_ix": normal((N_EVEN, LRU_BLOCKS, LRU_BLOCK_DIM, LRU_BLOCK_DIM), LRU_BLOCK_DIM ** -0.5),
        "lru_b_ix": normal((N_EVEN, LRU_WIDTH), 0.02),
        "lru_lambda": jnp.log(a_base / (1.0 - a_base)),
        "hyb_w_out": normal((N_EVEN, HYB_OUT, D_MODEL), HYB_OUT ** -0.5),
        "dif_w_qkv": normal((N_ODD, D_MODEL, 3 * DIFF_WIDTH), D_MODEL ** -0.5),
        "dif_lq1": normal((N_ODD, DIFF_HEAD_DIM), 0.1),
        "dif_lk1": normal((N_ODD, DIFF_HEAD_DIM), 0.1),
        "dif_lq2": normal((N_ODD, DIFF_HEAD_DIM), 0.1),
        "dif_lk2": normal((N_ODD, DIFF_HEAD_DIM), 0.1),
        "dif_subln": gain((N_ODD, 2 * DIFF_HEAD_DIM)),
        "dif_w_o": normal((N_ODD, DIFF_WIDTH, D_MODEL), DIFF_WIDTH ** -0.5),
        "final_norm": gain((D_MODEL,)),
    }

def reference(x, norm_ff1, ffn1_gate, ffn1_up, ffn1_down, norm_mix, norm_ff2, ffn2_gate, ffn2_up, ffn2_down,
              hyb_w_in, ssd_conv_w, ssd_conv_b, ssd_dt_bias, ssd_a_log, ssd_d, ssd_norm,
              lru_conv_w, lru_conv_b, lru_w_ra, lru_b_ra, lru_w_ix, lru_b_ix, lru_lambda, hyb_w_out,
              dif_w_qkv, dif_lq1, dif_lk1, dif_lq2, dif_lk2, dif_subln, dif_w_o, final_norm):
    cos, sin = rope_tables(x.shape[1])
    h = x
    for i in range(DEPTH):
        j = i // 2
        h = h + FFN_RES_SCALE * swiglu(rms_norm(h, norm_ff1[i]), ffn1_gate[i], ffn1_up[i], ffn1_down[i])
        hn = rms_norm(h, norm_mix[i])
        if i % 2 == 0:
            z, xbc, dt_raw, gate_b, x_b = jnp.split(hn @ hyb_w_in[j], HYB_SPLITS, axis=-1)
            y_a = ssd_mixer(z, xbc, dt_raw, ssd_conv_w[j], ssd_conv_b[j], ssd_dt_bias[j],
                            ssd_a_log[j], ssd_d[j], ssd_norm[j])
            y_b = rglru_mixer(gate_b, x_b, lru_conv_w[j], lru_conv_b[j], lru_w_ra[j], lru_b_ra[j],
                              lru_w_ix[j], lru_b_ix[j], lru_lambda[j])
            h = h + jnp.concatenate([y_a, y_b], axis=-1) @ hyb_w_out[j]
        else:
            lambda_init = 0.8 - 0.6 * math.exp(-0.3 * i)
            h = h + diff_attention(hn, dif_w_qkv[j], dif_lq1[j], dif_lk1[j], dif_lq2[j], dif_lk2[j],
                                   dif_subln[j], dif_w_o[j], lambda_init, cos, sin)
        h = h + FFN_RES_SCALE * swiglu(rms_norm(h, norm_ff2[i]), ffn2_gate[i], ffn2_up[i], ffn2_down[i])
    return rms_norm(h, final_norm)


_drawn_inputs = setup_inputs


def setup_inputs(seed=0):
    import zlib

    import numpy as np

    out = dict(_drawn_inputs(seed))
    spreads = {}
    factors = {'norm_ff1': 4.024,
     'norm_ff2': 5.881,
     'ssd_conv_b': 3.019,
     'ssd_d': 19.952,
     'ssd_norm': 14.018,
     'lru_b_ra': 200.0,
     'lru_b_ix': 200.0,
     'dif_lq2': 3.451,
     'dif_subln': 157.196,
     'final_norm': 20.721,
     'ssd_a_log': 30.16,
     'lru_conv_b': 45.232,
     'lru_lambda': 21.56,
     'lru_conv_w': 8.0,
     'lru_w_ra': 8.0,
     'lru_w_ix': 8.0}
    for name, (base, spread) in spreads.items():
        noise = np.random.default_rng([zlib.crc32(name.encode()), seed]).standard_normal(out[name].shape)
        drawn = base * np.exp(spread * noise) if base else spread * noise
        out[name] = __import__('jax').numpy.asarray(drawn.astype(out[name].dtype))
    for name, factor in factors.items():
        out[name] = (out[name] * factor).astype(out[name].dtype)
    return out
```

```python
import math
from contextlib import ExitStack

import numpy as np

import concourse.bass as bass
from concourse import mybir

P = 128
D, T, FF = 1024, 256, 2816
DT, FT = D // P, FF // P
TC = T // P
F32, F32R, BF16 = mybir.dt.float32, mybir.dt.float32r, mybir.dt.bfloat16
ALU, ACT, AX = mybir.AluOpType, mybir.ActivationFunctionType, mybir.AxisListType.X
EPS = 1e-6

RING = 4
KD = FT // 2
SLOT = KD * P

XBC, LW = 1536, 1024
NX, NL = XBC // P, LW // P
HEADS, HD = 16, 64
AH = 8
COL_Z, COL_XBC, COL_DT = 0, 1024, 2560
COL_GATE, COL_XB = 2576, 3600
LAMBDA_INIT = 0.8 - 0.6 * math.exp(-0.3 * 1)
MASKED = -3.0e38
SQRT_UP = 2.0 ** 40

PHASES = [("ffn", 0), ("hyb", 0), ("ffn", 1), ("ffn", 2), ("att", 0), ("ffn", 3)]
PAIRS = {"ffn": FT + DT, "hyb": 18 + DT, "att": 12 + DT // 2}

VEC, _at = {}, 0
for _name, _n in (("norm_ff1", 16), ("norm_mix", 16), ("norm_ff2", 16), ("final_norm", 8), ("ssd_conv_w", 4 * NX),
                  ("ssd_conv_b", NX), ("lru_conv_w", 4 * NL), ("lru_conv_b", NL), ("lru_b_ra", NL), ("lru_b_ix", NL),
                  ("lru_lambda", NL), ("ssd_norm", 8), ("ssd_d", 8), ("dif_subln", 1)):
    VEC[_name] = _at
    _at += _n
NVEC = _at
CON, _at = {}, 0
for _name, _n in (("ident", P), ("ones", P), ("tri", P), ("neg", P), ("rot", P), ("cos", T), ("sin", T)):
    CON[_name] = (_at, _at + _n)
    _at += _n
NCON = _at


def norm_weight(phases, n):
    if n == len(phases):
        return VEC["final_norm"]
    kind, i = phases[n]
    if kind == "ffn":
        return VEC["norm_ff1" if i % 2 == 0 else "norm_ff2"] + DT * (i // 2)
    return VEC["norm_mix"] + DT * (0 if kind == "hyb" else 1)


def trunk(nc, a, out, phases=PHASES):
    ctx = ExitStack()
    with ctx:
        def sb(name, shape, dt=F32):
            return ctx.enter_context(nc.sbuf_tensor(name, shape, dt))

        def sem(name):
            return ctx.enter_context(nc.semaphore(name))

        raw = sb("raw", [P, RING, SLOT])
        whi = sb("whi", [P, RING, SLOT], F32R)
        wlo = sb("wlo", [P, RING, SLOT], F32R)
        h = sb("h", [P, DT, T])
        xn = sb("xn", [P, DT, 2, T], F32R)
        hid = sb("hid", [P, FT, 2, T], F32R)
        rb = sb("rb", [P, T])
        rms = sb("rms", [P, T])
        sq = sb("sq", [P, T])
        sumsq = sb("sumsq", [P, T])
        vec = sb("vec", [P, NVEC])
        con = sb("con", [P, NCON])
        eps = sb("eps", [P, 1])
        arena = sb("arena", [P, 16272])
        small = sb("small", [P, 160])
        heads = sb("heads", [HEADS, 3])
        psum = ctx.enter_context(nc.psum_tensor("psum", [P, 8, 512], F32))
        banks = [psum[:, i, :] for i in range(8)]
        scores_ps = psum[:, 5:7, :]

        def cst(name):
            lo_, hi_ = CON[name]
            return con[:, lo_:hi_]

        ones = cst("ones")

        s_const = sem("s_const")
        s_x = sem("s_x")
        s_eps = sem("s_eps")
        s_raw = [sem(f"s_raw{i}") for i in range(RING)]
        s_whi = sem("s_whi")
        s_wlo = sem("s_wlo")
        s_blk = sem("s_blk")
        s_h = sem("s_h")
        s_xhi = sem("s_xhi")
        s_xlo = sem("s_xlo")
        s_sq = sem("s_sq")
        s_acc = sem("s_acc")
        s_stat = sem("s_stat")
        s_rms = sem("s_rms")
        s_rb = sem("s_rb")
        s_gu = sem("s_gu")
        s_silu = sem("s_silu")
        s_hu = sem("s_hu")
        s_hhi = sem("s_hhi")
        s_hlo = sem("s_hlo")
        s_fin = sem("s_fin")
        s_out = sem("s_out")

        first = [0]
        for kind, _ in phases:
            first.append(first[-1] + PAIRS[kind])

        def hidden_before(n):
            return FT * sum(1 for kind, _ in phases[:n] if kind == "ffn")

        SUMS = banks[2][:, 0:T]
        gu = arena[:, 0:1024].rearrange("p (b g t) -> p b g t", b=2, g=2)
        act_g = arena[:, 1024:1536].rearrange("p (b t) -> p b t", b=2)
        hu = arena[:, 1536:2048].rearrange("p (b t) -> p b t", b=2)
        rb2 = rb[:].unsqueeze(1).to_broadcast([P, 2, T])

        def tile_of(buf, s, k):
            return buf[:, s, 0:k * P].rearrange("p (k m) -> p k m", k=k)

        def load(sp, b, s, src, k, ring_full=True):
            if ring_full and not (isinstance(b, int) and b < RING):
                sp.wait_ge(s_wlo, b - RING + 1)
            sp.dma_start(tile_of(raw, s, k), src).then_inc(s_raw[s], 16)

        def split_hi(act, b, s, k, turn, ring_full=True):
            if ring_full and not (isinstance(b, int) and b < RING):
                act.wait_ge(s_blk, b - RING + 1)
            act.wait_ge(s_raw[s], turn * 16 + 16)
            act.activation(whi[:, s, 0:k * P], raw[:, s, 0:k * P], ACT.Copy).then_inc(s_whi, 1)

        def split_lo(dve, b, s, k):
            dve.wait_ge(s_whi, b + 1)
            dve.tensor_tensor(wlo[:, s, 0:k * P], raw[:, s, 0:k * P], whi[:, s, 0:k * P].bitcast(F32),
                              ALU.subtract).then_inc(s_wlo, 1)

        def multiply(pe, b, s, k, x, k0, acc, start=True, stop=True, need=None, part=None):
            pe.wait_ge(s_wlo, b + 1)
            for j in part or range(k):
                t = k0 + j
                if need:
                    need(t)
                w_hi, w_lo = tile_of(whi, s, k)[:, j, :], tile_of(wlo, s, k)[:, j, :]
                pe.matmul(acc, w_hi, x[:, t, 0, :], start=start and j == 0, stop=False)
                pe.matmul(acc, w_hi, x[:, t, 1, :], start=False, stop=False)
                mm = pe.matmul(acc, w_lo, x[:, t, 0, :], start=False, stop=stop and j == k - 1)
            if j == k - 1:
                mm.then_inc(s_blk, 1)

        def half(pair, m):
            return banks[pair % 2][:, m * T:(m + 1) * T]

        def both(pair):
            return banks[pair % 2][:, :].rearrange("p (g t) -> p g t", g=2)

        def convert_hi(act, pair, k, ring_full=True, blocks=2):
            for b in (2 * pair, 2 * pair + 1)[:blocks]:
                split_hi(act, b, b % RING, k, b // RING, ring_full)

        def convert_lo(dve, pair, k, hi_of_second=False):
            b = 2 * pair
            split_lo(dve, b, b % RING, k)
            b += 1
            if hi_of_second:
                s = b % RING
                dve.wait_ge(s_blk, b - RING + 1)
                dve.wait_ge(s_raw[s], b // RING * 16 + 16)
                dve.tensor_copy(whi[:, s, 0:k * P], raw[:, s, 0:k * P]).then_inc(s_whi, 1)
            split_lo(dve, b, b % RING, k)

        def read_out(eng, pair):
            if pair < 0:
                return
            n = max(m for m in range(len(phases)) if first[m] <= pair)
            kind, j = phases[n][0], pair - first[n]
            inner = {"ffn": FT, "hyb": 18, "att": 12}[kind]
            if j >= inner:
                eng.wait_ge(s_h, DT * n + (j - inner + 1) * (2 if kind == "att" else 1))
            elif kind == "ffn":
                eng.wait_ge(s_gu, hidden_before(n) + j + 1)
            else:
                eng.wait_ge(s_pr if kind == "hyb" else s_qkv, j + 1)

        def fresh(eng, n, d):
            if n == 0:
                eng.wait_ge(s_x, 16)
            else:
                eng.wait_ge(s_h, DT * (n - 1) + d + 1)

        def residual_hi(act, n, d):
            if n == len(phases):
                return
            fresh(act, n, d)
            w = norm_weight(phases, n) + d
            act.activation(xn[:, d, 0, :], h[:, d, :], ACT.Copy, scale=vec[:, w:w + 1]).then_inc(s_xhi, 1)

        def residual_lo(dve, n, d):
            if n == len(phases):
                return
            dve.wait_ge(s_xhi, DT * n + d + 1)
            w = norm_weight(phases, n) + d
            dve.scalar_tensor_tensor(xn[:, d, 1, :], h[:, d, :], vec[:, w:w + 1],
                                     xn[:, d, 0, :].bitcast(F32), ALU.mult, ALU.subtract).then_inc(s_xlo, 1)

        def residual_square(pool, n, d):
            fresh(pool, n, d)
            if d == 0:
                if n:
                    pool.wait_ge(s_stat, n)
                pool.tensor_tensor(sumsq[:], h[:, d, :], h[:, d, :], ALU.mult).then_inc(s_acc, 1)
                return
            pool.wait_ge(s_acc, DT * n + d)
            pool.tensor_tensor(sq[:], h[:, d, :], h[:, d, :], ALU.mult).then_inc(s_sq, 1)
            pool.wait_ge(s_sq, (DT - 1) * n + d)
            pool.tensor_tensor(sumsq[:], sumsq[:], sq[:], ALU.add).then_inc(s_acc, 1)

        def token_sums(pe, n):
            pe.wait_ge(s_acc, DT * (n + 1))
            if n:
                pe.wait_ge(s_rms, n)
            pe.matmul(SUMS, ones, sumsq[:], start=True, stop=True).then_inc(s_stat, 1)

        def token_rms(act, n):
            act.wait_ge(s_stat, n + 1)
            if n:
                act.wait_ge(s_rb, n)
            act.activation(rms[:], SUMS, ACT.Sqrt, scale=1.0 / D, bias=eps[:, 0:1]).then_inc(s_rms, 1)

        def token_scale(dve, n):
            dve.wait_ge(s_rms, n + 1)
            dve.reciprocal(rb[:], rms[:]).then_inc(s_rb, 1)
            dve.wait_ge(s_rb, n + 1)

        def add_residual(dve, n, d, acc, scale):
            dve.wait_ge(s_acc, DT * n + d + 1)
            dve.scalar_tensor_tensor(h[:, d, :], acc, scale, h[:, d, :], ALU.mult, ALU.add).then_inc(s_h, 1)
            dve.wait_ge(s_h, DT * n + d + 1)
            residual_lo(dve, n + 1, d)

        def ffn_matrices(i):
            pre = "ffn1" if i % 2 == 0 else "ffn2"
            return [a[f"{pre}_{m}"][i // 2] for m in ("gate", "up", "down")]

        def ffn_sync(sp, n, i):
            gate, up, down = ffn_matrices(i)
            b0 = 2 * first[n]

            def gate_up(it, ring_full):
                for s in range(RING):
                    c = it * (2 * P) + (s // 2) * P
                    load(sp, it * RING + (b0 + s), s,
                         (gate, up)[s % 2][:, bass.ds(c, P)].rearrange("(k p) m -> p k m", p=P), DT, ring_full)

            if n == 0:
                gate_up(0, False)
            with sp.Fori(1 if n == 0 else 0, FT // 2) as it:
                gate_up(it, True)
            with sp.Fori(0, DT // 2) as it:
                for s in range(RING):
                    rows = down[(s % 2) * KD * P:(s % 2 + 1) * KD * P, :]
                    load(sp, it * RING + (b0 + 2 * FT + s), s,
                         rows[:, bass.ds(it * (2 * P) + (s // 2) * P, P)].rearrange("(k p) m -> p k m", p=P), KD)

        def ffn_tensor(pe, n, i):
            p0, p1, hb = first[n], first[n] + FT, hidden_before(n)

            def gate_up(p, g, need=None):
                for m in range(2):
                    multiply(pe, p * 2 + m, 2 * g + m, DT, xn, 0, half(g, m), need=need if m == 0 else None)

            def down(p, g, need=None):
                for m in range(2):
                    multiply(pe, p * 2 + m, 2 * g + m, KD, hid, m * KD, half(g, 0), start=m == 0, stop=m == 1,
                             need=need)

            if n:
                read_out(pe, p0 - 2)
            gate_up(p0, 0, lambda t: pe.wait_ge(s_xlo, DT * n + t + 1))
            token_sums(pe, n)
            if n:
                read_out(pe, p0 - 1)
            gate_up(p0 + 1, 1)
            with pe.Fori(1, FT // 2) as it:
                for g in range(2):
                    pe.wait_ge(s_gu, it * 2 + (hb + g - 1))
                    gate_up(it * 2 + (p0 + g), g)
            read_out(pe, p1 - 2)
            down(p1, 0, lambda t: pe.wait_ge(s_hlo, hb + t + 1))
            read_out(pe, p1 - 1)
            down(p1 + 1, 1)
            with pe.Fori(1, DT // 2) as it:
                for g in range(2):
                    pe.wait_ge(s_h, it * 2 + (DT * n + g - 1))
                    down(it * 2 + (p1 + g), g)

        def ffn_scalar(act, n, i, before):
            p0, t0, hb = first[n], 2 * first[n] // RING, hidden_before(n)

            def silu(q, g):
                act.wait_ge(s_gu, q + 1)
                act.activation(act_g[:, g, :], gu[:, g, 0, :], ACT.Silu).then_inc(s_silu, 1)

            def hidden_hi(q, g, j):
                act.wait_ge(s_hu, q + 1)
                act.activation(hid[:, bass.ds(j, 1), 0, :].rearrange("p a t -> p (a t)"), hu[:, g, :],
                               ACT.Copy).then_inc(s_hhi, 1)

            for g in range(2):
                before[g]()
                convert_hi(act, p0 + g, DT, n > 0)
            token_rms(act, n)
            with act.Fori(1, FT // 2) as it:
                for g in range(2):
                    silu(it * 2 + (hb - 2 + g), g)
                    for m in range(2):
                        split_hi(act, it * 4 + (2 * p0 + 2 * g + m), 2 * g + m, DT, it + t0)
                    hidden_hi(it * 2 + (hb - 2 + g), g, it * 2 + (g - 2))
            for e in range(DT):
                if e < 2:
                    silu(hb + FT - 2 + e, e)
                    hidden_hi(hb + FT - 2 + e, e, FT - 2 + e)
                else:
                    residual_hi(act, n + 1, e - 2)
                convert_hi(act, p0 + FT + e, KD)
            return [lambda: residual_hi(act, n + 1, DT - 2), lambda: residual_hi(act, n + 1, DT - 1)]

        def ffn_vector(dve, n, i, before):
            p0, hb = first[n], hidden_before(n)

            def scale(p, q, g, early=False):
                dve.wait_ge(s_blk, p * 2 + 2)
                if not early:
                    dve.wait_ge(s_hlo, q - 1)
                dve.tensor_tensor(gu[:, g, :, :], both(g), rb2, ALU.mult).then_inc(s_gu, 1)

            def product(q, g):
                dve.wait_ge(s_gu, q + 1)
                dve.wait_ge(s_silu, q + 1)
                dve.tensor_tensor(hu[:, g, :], act_g[:, g, :], gu[:, g, 1, :], ALU.mult).then_inc(s_hu, 1)

            def hidden_lo(q, g, j):
                dve.wait_ge(s_hhi, q + 1)
                v = hid[:, bass.ds(j, 1), :, :].rearrange("p a b t -> p (a b) t")
                dve.tensor_tensor(v[:, 1, :], hu[:, g, :], v[:, 0, :].bitcast(F32), ALU.subtract).then_inc(s_hlo, 1)

            def step(it, g, early=False):
                q = it * 2 + (hb - 2 + g)
                scale(it * 2 + (p0 - 2 + g), q, g, early)
                split_lo(dve, it * 4 + (2 * p0 + 2 * g), 2 * g, DT)
                product(q, g)
                split_lo(dve, it * 4 + (2 * p0 + 2 * g + 1), 2 * g + 1, DT)
                hidden_lo(q, g, it * 2 + (g - 2))

            for g in range(2):
                before[g]()
                convert_lo(dve, p0 + g, DT)
            token_scale(dve, n)
            if n == 0:
                for g in range(2):
                    step(1, g, True)
            with dve.Fori(2 if n == 0 else 1, FT // 2) as it:
                for g in range(2):
                    step(it, g)
            for e in range(DT):
                if e < 2:
                    q = hb + FT - 2 + e
                    scale(p0 + FT - 2 + e, q, e)
                    product(q, e)
                    hidden_lo(q, e, FT - 2 + e)
                else:
                    down_out(dve, n, e - 2)
                convert_lo(dve, p0 + FT + e, KD)
            return [lambda: down_out(dve, n, DT - 2), lambda: down_out(dve, n, DT - 1)]

        def down_out(dve, n, d):
            p = first[n] + FT + d
            dve.wait_ge(s_blk, 2 * p + 2)
            add_residual(dve, n, d, half(p, 0), 0.5)

        s_hw = sem("s_hw")
        s_zero = sem("s_zero")
        s_wdt = sem("s_wdt")
        s_pr = sem("s_pr")
        s_cv = sem("s_cv")
        s_tap = sem("s_tap")
        s_xc = sem("s_xc")
        s_dtp = sem("s_dtp")
        s_spx = sem("s_spx")
        s_spe = sem("s_spe")
        s_spu = sem("s_spu")
        s_spl = sem("s_spl")
        s_sp = sem("s_sp")
        s_cs = sem("s_cs")
        s_tokp = sem("s_tokp")
        s_tok = sem("s_tok")
        s_cbp = sem("s_cbp")
        s_cb = sem("s_cb")
        s_xtp = sem("s_xtp")
        s_xt = sem("s_xt")
        s_csb = sem("s_csb")
        s_seg = sem("s_seg")
        s_dec = sem("s_dec")
        s_m = sem("s_m")
        s_y = sem("s_y")
        s_yr = sem("s_yr")
        s_sz = sem("s_sz")
        s_yg = sem("s_yg")
        s_ysq = sem("s_ysq")
        s_ysum = sem("s_ysum")
        s_yrms = sem("s_yrms")
        s_yrb = sem("s_yrb")
        s_ybc = sem("s_ybc")
        s_yn = sem("s_yn")
        s_gp = sem("s_gp")
        s_gs = sem("s_gs")
        s_ix = sem("s_ix")
        s_at = sem("s_at")
        s_v = sem("s_v")
        s_mu = sem("s_mu")
        s_hl = sem("s_hl")
        s_gl = sem("s_gl")
        s_yb = sem("s_yb")
        s_yhi = sem("s_yhi")
        s_ylo = sem("s_ylo")
        s_bhi = sem("s_bhi")
        s_blo = sem("s_blo")

        def grid(at, n, width=T):
            return arena[:, at:at + n * width].rearrange("p (n t) -> p n t", n=n)

        xbc = grid(0, NX)
        xtok = grid(3072, TC, LW)
        sz = grid(5120, NL)
        lh = grid(7168, NL)
        lrw = arena[:, 7168:9216].rearrange("p (t g m) -> p t g m", t=NL, g=2)
        lx_hi = grid(9216, 4)
        lr, li, la = grid(10240, 4), grid(11264, 4), grid(12288, 4)
        pad = arena[:, 13312:13312 + 4 * (T + 3)].rearrange("p (b m t) -> p b m t", b=2, m=2)
        cbm = grid(14348, 2, 3 * P)
        seg = grid(15116, 2, 3 * P)
        seg_z = grid(6400, 2, 3 * P)
        seg_p = grid(13312, 2, 3 * P)
        wdt = arena[:, 15884:16012].rearrange("p (k m) -> p k m", k=DT)
        cs = arena[0:HEADS, 16012:16268]
        row = [arena[0:HEADS, 9216 + T * k:9216 + T * (k + 1)] for k in range(16)]
        X_, E_, U_, L_, D_, M_, DTR, DTA, NCS, ECS = row[:10]
        tok = small[:, 0:80]
        lam8 = small[:, 80:88]
        lt = [small[:, 88 + 8 * k:96 + 8 * k] for k in range(6)]
        arms = small[:, 136:138]
        yrms = small[:, 150:154].rearrange("p (g c) -> p g c", g=2)
        yrb = small[:, 154:158].rearrange("p (g c) -> p g c", g=2)
        ident, tri = cst("ident"), cst("tri")

        def seg_of(hd):
            m = hd // 2
            return (seg if m % 2 == 0 else seg_z if m < 4 else seg_p)[:, hd % 2, :]

        def gate_of(k):
            return xbc[:, 8 + 2 * k:10 + 2 * k, :] if k < 2 else sz[:, 2 * k - 4:2 * k - 2, :]

        def lx(t):
            return xbc[:, 8 + t, :] if t < 4 else lx_hi[:, t - 4, :]

        CONV = [8, 9, 10, 11, 0, 1, 2, 3, 4, 5, 6, 7]

        ROUNDED_BY_VECTOR = (15, 16, 17)
        OUT_BLOCKS = [(0, 0), (1, 0), (0, 1), (1, 1)] + [(d, q) for d in range(2, DT) for q in range(2)]

        def column(name, c):
            return vec[:, VEC[name] + c:VEC[name] + c + 1]

        def conv_tile(ct):
            if ct < NX:
                return xbc[:, CONV[ct], :], "ssd_conv", NX, CONV[ct]
            return lx(ct - NX), "lru_conv", NL, ct - NX

        def hyb_weights(pool):
            pool.memset(arena[:, 7168:9216], 0.0).then_inc(s_zero, 1)
            pool.wait_ge(s_zero, 1)
            for g, name in enumerate(("lru_w_ra", "lru_w_ix")):
                w = a[name][0].rearrange("(t q) i j -> q i t j", q=2)
                for q in range(2):
                    pool.dma_start(lrw[64 * q:64 * q + 64, :, g, 64 * q:64 * q + 64], w[q]).then_inc(s_hw, 16)
            pool.dma_start(wdt, a["hyb_w_in"][0][:, COL_DT:COL_DT + HEADS].rearrange("(k p) m -> p k m", p=P)
                           ).then_inc(s_hw, 16)

        def hyb_sync(sp, n, i):
            b = 2 * first[n]
            w_in, w_out = a["hyb_w_in"][0], a["hyb_w_out"][0]
            cols = [COL_XBC + P * t for t in CONV] + [COL_XB + P * t for t in range(NL)]
            cols += [COL_Z + P * t for t in range(NL)] + [COL_GATE + P * t for t in range(NL)]
            for c in cols:
                load(sp, b, b % RING, w_in[:, c:c + P].rearrange("(k p) m -> p k m", p=P), DT)
                b += 1
            for d, q in OUT_BLOCKS:
                load(sp, b, b % RING, w_out[q * LW:(q + 1) * LW, d * P:(d + 1) * P]
                     .rearrange("(k p) m -> p k m", p=P), DT)
                b += 1

        def hyb_tensor(pe, n, i):
            p0 = first[n]

            def dt_product():
                pe.wait_ge(s_wdt, 1)
                for k in range(DT):
                    mm = pe.matmul(banks[3][0:HEADS, 0:T], wdt[:, k, :], h[:, k, :], start=k == 0, stop=k == DT - 1)
                mm.then_inc(s_dtp, 1)

            def rows_to_tokens():
                pe.wait_ge(s_cs, 1)
                for k, r in enumerate((DTR[:, 0:P], DTR[:, P:T], NCS[:, 0:P], NCS[:, P:T], ECS[:, 0:P])):
                    mm = pe.transpose(banks[3][:, 16 * k:16 * k + 16], r, ident[0:HEADS, 0:HEADS])
                mm.then_inc(s_tokp, 1)

            def c_dot_b():
                pe.wait_ge(s_xc, 4)
                for g in range(2):
                    bm, cm, out_ = xbc[:, 8 + g, :], xbc[:, 10 + g, :], banks[6 + g]
                    pe.matmul(out_[:, 0:T], bm[:, 0:P], cm, start=True, stop=True)
                    pe.matmul(out_[:, T:T + P], bm[:, P:T], cm[:, P:T], start=True, stop=True).then_inc(s_cbp, 1)

            def x_to_tokens(g):
                pe.wait_ge(s_xc, 6 + 2 * g)
                if g >= 2:
                    pe.wait_ge(s_xt, g - 1)
                for c in range(TC):
                    for m in range(2):
                        mm = pe.transpose(banks[(4, 2)[g % 2]][:, (2 * c + m) * P:(2 * c + m + 1) * P],
                                          xbc[:, 2 * g + m, c * P:(c + 1) * P], ident)
                mm.then_inc(s_xtp, 1)

            def broadcast_cs(hd):
                pe.wait_ge(s_seg, hd - 1) if hd >= 2 else pe.wait_ge(s_cb, 2)
                pe.matmul(banks[5 + 2 * (hd % 2)][:, 0:T], ident[0:HEADS, hd:hd + 1].to_broadcast([HEADS, P]), cs,
                          start=True, stop=True).then_inc(s_csb, 1)

            def head_y(hd):
                t, q = hd // 2, hd % 2
                pe.wait_ge(s_m, hd + 1)
                pe.wait_ge(s_xt, t // 2 + 1)
                if t and q == 0:
                    pe.wait_ge(s_yr, t)
                o = banks[6][64 * q:64 * q + 64, :]
                v = seg_of(hd)
                pe.matmul(o[:, 0:T], xtok[:, 0, HD * hd:HD * hd + HD], v[:, 0:T], start=True, stop=False)
                pe.matmul(o[:, P:T], xtok[:, 1, HD * hd:HD * hd + HD], v[:, T:3 * P], start=False,
                          stop=True).then_inc(s_y, 1)

            def lru_gates(t):
                if t == 0:
                    pe.wait_ge(s_hw, 80)
                pe.wait_ge(s_tap, 3 * (NX + t - t % 2) + 5 + t % 2)
                if t == 0:
                    pe.wait_ge(s_xt, 4)
                if t >= 2:
                    pe.wait_ge(s_gs, 2 * (t - 1))
                o = banks[3 + t % 2]
                pe.matmul(o[:, 0:T], lrw[:, t, 0, :], lx(t), start=True, stop=True)
                pe.matmul(o[:, T:2 * T], lrw[:, t, 1, :], lx(t), start=True, stop=True).then_inc(s_gp, 1)

            def group_sums(g):
                pe.wait_ge(s_ysq, 2 * g + 2)
                if g:
                    pe.wait_ge(s_gs, 2 * NL)
                for c in range(TC):
                    for k in range(4):
                        mm = pe.matmul(banks[2 + g][:, T + c:T + c + 1],
                                       sz[:, 4 * g + k, c * P:(c + 1) * P], ones[:, 0:1], start=k == 0, stop=k == 3)
                mm.then_inc(s_ysum, 1)

            def group_scale(g):
                pe.wait_ge(s_yrb, g + 1)
                if g:
                    pe.wait_ge(s_yn, 4)
                for c in range(TC):
                    mm = pe.matmul(banks[2][:, c * P:(c + 1) * P], yrb[:, g, c:c + 1].to_broadcast([P, P]), ident,
                                   start=True, stop=True)
                mm.then_inc(s_ybc, 1)

            after = {s: [] for s in range(18)}
            after[0] += [dt_product]
            after[5] += [c_dot_b]
            after[6] += [rows_to_tokens]
            for g, s in enumerate((6, 6, 7, 8)):
                after[s] += [lambda g=g: x_to_tokens(g)]
            for m in range(8):
                after[6 + m] += [lambda m=m: broadcast_cs(2 * m), lambda m=m: broadcast_cs(2 * m + 1)]
                after[8 + m] += [lambda m=m: head_y(2 * m), lambda m=m: head_y(2 * m + 1)]
            for k, s in enumerate((9, 10, 13, 14)):
                after[s] += [lambda k=k: lru_gates(2 * k), lambda k=k: lru_gates(2 * k + 1)]
            after[14] += [lambda: group_sums(0)]
            after[16] += [lambda: group_scale(0)]
            after[16] += [lambda: group_sums(1)]
            after[17] += [lambda: group_scale(1)]
            for j in range(18):
                read_out(pe, p0 + j - 2)
                for m in range(2):
                    b = 2 * (p0 + j) + m
                    multiply(pe, b, b % RING, DT, xn, 0, half(p0 + j, m),
                             need=(lambda t: pe.wait_ge(s_xlo, DT * n + t + 1)) if j + m == 0 else None)
                if j == 0:
                    token_sums(pe, n)
                for task in after[j]:
                    task()
            def ready(t):
                pe.wait_ge(s_ylo if t < 8 else s_blo, t % 8 + 1)

            for k, (d, q) in enumerate(OUT_BLOCKS):
                if q == 0:
                    read_out(pe, p0 + 16 + d)
                b = 2 * (p0 + 18) + k
                multiply(pe, b, b % RING, DT, hid, 8 * q, half(p0 + 18 + d, 0), start=q == 0, stop=q == 1,
                         need=ready if d == 0 else None)

        def hyb_scalar(act, n, i, before):
            p0 = first[n]

            def conv_first(j):
                act.wait_ge(s_pr, j + 1)
                for m in range(2):
                    o, name, _, c = conv_tile(2 * j + m)
                    k3 = (NX if name == "ssd_conv" else NL) * 3
                    act.activation(o, pad[:, j % 2, m, 3:3 + T], ACT.Identity, scale=column(name + "_w", k3 + c),
                                   bias=column(name + "_b", c)).then_inc(s_cv, 1)

            def conv_silu(j):
                for m in range(2):
                    act.wait_ge(s_tap, 6 * j + 5 + m)
                    o = conv_tile(2 * j + m)[0]
                    act.activation(o, o, ACT.Silu).then_inc(s_xc, 1)

            def softplus_exp():
                act.wait_ge(s_spx, 2)
                act.activation(E_, X_, ACT.Abs).then_inc(s_spe, 1)
                act.activation(lt[1], lt[0], ACT.Abs).then_inc(s_spe, 1)
                act.wait_ge(s_spe, 2)
                act.activation(E_, E_, ACT.Exp, scale=-1.0).then_inc(s_spe, 1)
                act.activation(lt[1], lt[1], ACT.Exp, scale=-1.0).then_inc(s_spe, 1)
                act.activation(arms[0:HEADS, 0:1], heads[:, 1:2], ACT.Exp).then_inc(s_spe, 1)

            def softplus_ln():
                act.wait_ge(s_spu, 2)
                act.activation(L_, U_, ACT.Ln).then_inc(s_spl, 1)
                act.activation(lt[3], lt[2], ACT.Ln).then_inc(s_spl, 1)

            def decay(hd):
                act.wait_ge(s_seg, hd + 1)
                act.activation(seg_of(hd), seg_of(hd), ACT.Exp).then_inc(s_dec, 1)

            def gates(t):
                act.wait_ge(s_gp, t + 1)
                if t == 4:
                    act.wait_ge(s_hl, 4)
                o = banks[3 + t % 2]
                act.activation(lr[:, t % 4, :], o[:, 0:T], ACT.Sigmoid, bias=column("lru_b_ra", t)).then_inc(s_gs, 1)
                act.activation(li[:, t % 4, :], o[:, T:2 * T], ACT.Sigmoid,
                               bias=column("lru_b_ix", t)).then_inc(s_gs, 1)

            def decays_of_lru(k):
                act.wait_ge(s_gs, 8 * k + 8)
                for t in range(4 * k, 4 * k + 4):
                    act.activation(la[:, t % 4, :], lr[:, t % 4, :], ACT.Exp, scale=nlam8[:, t:t + 1]).then_inc(s_at, 1)
                act.wait_ge(s_at, 8 * k + 4)
                for t in range(4 * k, 4 * k + 4):
                    act.activation(lr[:, t % 4, :], lr[:, t % 4, :], ACT.Tanh, scale=lam8[:, t:t + 1]).then_inc(s_at, 1)

            def mult_of_lru(k):
                act.wait_ge(s_v, 3 * k + 2)
                act.activation(lr[:, :, :], lr[:, :, :], ACT.Sqrt, scale=SQRT_UP).then_inc(s_mu, 1)

            def silu_z(k):
                act.wait_ge(s_pr, 12 + 2 * k)
                v = sz[:, 4 * k:4 * k + 4, :]
                act.activation(v, v, ACT.Silu).then_inc(s_sz, 1)

            def gelu(k):
                act.wait_ge(s_pr, 15 + k)
                v = gate_of(k)
                act.activation(v, v, ACT.Gelu_apprx_tanh).then_inc(s_gl, 1)

            def lru_hi(k):
                act.wait_ge(s_yb, k + 1)
                for m in range(2):
                    act.activation(hid[:, 8 + 2 * k + m, 0, :], gate_of(k)[:, m, :], ACT.Copy).then_inc(s_bhi, 1)

            def group_rms(g):
                act.wait_ge(s_ysum, g + 1)
                act.activation(yrms[:, g, :], banks[2 + g][:, T:T + TC], ACT.Sqrt, scale=1.0 / 512,
                               bias=eps[:, 0:1]).then_inc(s_yrms, 1)

            def y_hi(t):
                act.wait_ge(s_yn, t + 1)
                act.activation(hid[:, t, 0, :], xbc[:, t, :], ACT.Copy).then_inc(s_yhi, 1)

            todo = {s: [] for s in range(20)}
            for j in range(6):
                todo[j + 3] += [lambda j=j: conv_silu(j)]
            todo[16] += [lambda: gates(6), lambda: gates(7)]
            for m in range(8):
                todo[9 + m] += [lambda m=m: decay(2 * m), lambda m=m: decay(2 * m + 1)]
            todo[15] += [lambda: silu_z(1)]
            for j in range(10):
                todo[j + 2] += [lambda j=j: conv_first(j)]
            todo[2] += [softplus_exp]
            todo[3] += [softplus_ln]
            for k, s in enumerate((11, 12, 15)):
                todo[s] += [lambda k=k: gates(2 * k), lambda k=k: gates(2 * k + 1)]
            todo[12] += [lambda: decays_of_lru(0)]
            todo[13] += [lambda: silu_z(0)]
            todo[14] += [lambda: mult_of_lru(0)]
            todo[16] += [lambda: decays_of_lru(1)]
            todo[17] += [lambda: gelu(0), lambda: group_rms(0)]
            todo[18] += [lambda: group_rms(1), lambda: mult_of_lru(1), lambda: gelu(1)]
            todo[18] += [lambda: lru_hi(0)] + [lambda t=t: y_hi(t) for t in range(4)]
            todo[19] += [lambda t=t: y_hi(t) for t in range(4, 8)] + [lambda: lru_hi(1), lambda: gelu(2), lambda: gelu(3)]
            for s in range(20):
                if s < 2:
                    before[s]()
                if s - 1 in ROUNDED_BY_VECTOR:
                    act.wait_ge(s_wlo, 2 * (p0 + s))
                convert_hi(act, p0 + s, DT, blocks=1 if s in ROUNDED_BY_VECTOR else 2)
                if s == 1:
                    token_rms(act, n)
                for task in todo[s]:
                    task()
            for k in (2, 3):
                lru_hi(k)
            for s in range(20, 26):
                residual_hi(act, n + 1, s - 20)
                convert_hi(act, p0 + s, DT)
            return [lambda: residual_hi(act, n + 1, DT - 2), lambda: residual_hi(act, n + 1, DT - 1)]

        nlam8 = small[:, 138:146]

        def hyb_vector(dve, n, i, before):
            p0 = first[n]
            links = [0]

            def link(ins):
                ins.then_inc(s_sp, 1)
                links[0] += 1
                dve.wait_ge(s_sp, links[0])

            def scaled(j, dst):
                dve.wait_ge(s_blk, 2 * (p0 + j) + 2)
                dve.tensor_tensor(dst, both(p0 + j), rb2, ALU.mult).then_inc(s_pr, 1)

            def conv_taps(j):
                for k in (2, 1, 0):
                    for m in range(2):
                        o, name, step, c = conv_tile(2 * j + m)
                        if j == 0:
                            dve.wait_ge(s_wdt, 2)
                        if k == 2:
                            dve.wait_ge(s_cv, 2 * j + m + 1)
                        else:
                            dve.wait_ge(s_tap, 6 * j + 2 * (2 - k) + m - 1)
                        dve.scalar_tensor_tensor(o, pad[:, j % 2, m, k:k + T], column(name + "_w", k * step + c), o,
                                                 ALU.mult, ALU.add).then_inc(s_tap, 1)

            def dt_weights():
                dve.wait_ge(s_hw, 80)
                w = norm_weight(phases, n)
                dve.tensor_tensor(wdt, wdt, vec[:, w:w + DT].unsqueeze(2).to_broadcast([P, DT, HEADS]),
                                  ALU.mult).then_inc(s_wdt, 1)
                dve.memset(pad[:, :, :, 0:3], 0.0).then_inc(s_wdt, 1)

            def softplus_args():
                dve.wait_ge(s_dtp, 1)
                link(dve.tensor_tensor(X_, banks[3][0:HEADS, 0:T], rb[0:HEADS, :], ALU.mult))
                dve.tensor_scalar(X_, X_, heads[:, 0:1], None, ALU.add).then_inc(s_spx, 1)
                dve.tensor_scalar(lt[0], vec[:, VEC["lru_lambda"]:VEC["lru_lambda"] + NL], -1.0, None,
                                  ALU.mult).then_inc(s_spx, 1)

            def softplus_u():
                dve.wait_ge(s_spe, 5)
                dve.tensor_scalar(U_, E_, 1.0, None, ALU.add).then_inc(s_spu, 1)
                dve.tensor_scalar(lt[2], lt[1], 1.0, None, ALU.add).then_inc(s_spu, 1)
                dve.wait_ge(s_spu, 2)

            def softplus_ratio(u, d, m):
                link(dve.tensor_scalar(d, u, -1.0, None, ALU.add))
                link(dve.tensor_scalar(m, d, 0.0, None, ALU.is_equal))
                link(dve.tensor_tensor(d, d, m, ALU.add))
                link(dve.reciprocal(d, d))

            def softplus_end(x, e, l, d, m, out_):
                link(dve.tensor_tensor(l, l, m, ALU.add))
                link(dve.tensor_tensor(e, e, d, ALU.mult))
                link(dve.tensor_tensor(l, l, e, ALU.mult))
                link(dve.scalar_tensor_tensor(out_, x, 0.0, l, ALU.max, ALU.add))

            def steps_of_dt():
                dve.wait_ge(s_spl, 2)
                softplus_end(X_, E_, L_, D_, M_, DTR)
                link(dve.tensor_scalar(DTA, DTR, arms[0:HEADS, 0:1], -1.0, ALU.mult, ALU.mult))

            def scale_of_lambda():
                softplus_ratio(lt[2], lt[4], lt[5])
                softplus_end(lt[0], lt[1], lt[3], lt[4], lt[5], lam8)
                link(dve.tensor_scalar(lam8, lam8, 8.0, None, ALU.mult))
                link(dve.tensor_scalar(nlam8, lam8, -1.0, None, ALU.mult))

            def sums_of_dt():
                for c in range(TC):
                    link(dve.tensor_tensor_scan(cs[:, c * P:(c + 1) * P], ones[0:HEADS, :], DTA[:, c * P:(c + 1) * P],
                                                0.0, ALU.mult, ALU.add))
                link(dve.tensor_scalar(NCS, cs, -1.0, None, ALU.mult))
                dve.tensor_scalar(ECS[:, 0:P], cs[:, 0:P], -1.0, cs[:, P - 1:P], ALU.mult, ALU.add).then_inc(s_cs, 1)

            def take_tok():
                dve.wait_ge(s_tokp, 1)
                dve.tensor_copy(tok, banks[3][:, 0:80]).then_inc(s_tok, 1)
                dve.wait_ge(s_tok, 1)

            def take_cb(g):
                dve.wait_ge(s_cbp, g + 1)
                for c in (0, 2):
                    link(dve.tensor_tensor(cbm[:, g, c * P:(c + 1) * P], banks[6 + g][:, c * P:(c + 1) * P], tri,
                                           ALU.mult))
                dve.tensor_copy(cbm[:, g, P:T], banks[6 + g][:, P:T]).then_inc(s_cb, 1)

            def take_x(g):
                dve.wait_ge(s_xtp, g + 1)
                src = banks[(4, 2)[g % 2]][:, :].rearrange("p (c q e) -> p c q e", c=TC, q=4)
                dts = tok[:, 0:32].rearrange("p (c q) -> p c q", c=TC)[:, :, 4 * g:4 * g + 4]
                dst = xtok[:, :, 4 * g * HD:(4 * g + 4) * HD].rearrange("p c (q e) -> p c q e", q=4)
                dve.tensor_tensor(dst, src, dts.unsqueeze(3).to_broadcast([P, TC, 4, HD]), ALU.mult).then_inc(s_xt, 1)

            def exponents(hd):
                dve.wait_ge(s_csb, hd + 1)
                if hd >= 4:
                    dve.wait_ge(s_y, hd - 3)
                if hd == 8:
                    dve.wait_ge(s_tap, 3 * (NX + NL))
                c, v = banks[5 + 2 * (hd % 2)], seg_of(hd)
                dve.tensor_scalar(v[:, 0:P], c[:, 0:P], tok[:, 32 + hd:33 + hd], 0.0, ALU.add, ALU.min)
                dve.tensor_scalar(v[:, P:T], c[:, P:T], tok[:, 64 + hd:65 + hd], None, ALU.add)
                dve.tensor_scalar(v[:, T:3 * P], c[:, P:T], tok[:, 48 + hd:49 + hd], 0.0, ALU.add,
                                  ALU.min).then_inc(s_seg, 1)

            def take_y(t):
                dve.wait_ge(s_y, 2 * t + 2)
                dve.scalar_tensor_tensor(xbc[:, t, :], xbc[:, t, :], column("ssd_d", t), banks[6][:, 0:T], ALU.mult,
                                         ALU.add).then_inc(s_yr, 1)

            def lru_mult2(k):
                dve.wait_ge(s_at, 8 * k + 8)
                dve.wait_ge(s_ix, k + 1)
                t = lxb(k)
                dve.tensor_tensor(t, la[:, :, :], la[:, :, :], ALU.mult).then_inc(s_v, 1)
                dve.wait_ge(s_v, 3 * k + 1)
                dve.scalar_tensor_tensor(lr[:, :, :], t, 1.0, lr[:, :, :], ALU.add, ALU.mult).then_inc(s_v, 1)

            def lru_scan(k):
                dve.wait_ge(s_mu, k + 1)
                dve.scalar_tensor_tensor(li[:, :, :], lr[:, :, :], SQRT_UP ** -0.5, li[:, :, :], ALU.mult,
                                         ALU.mult).then_inc(s_v, 1)
                dve.wait_ge(s_v, 3 * k + 3)
                for t in range(4 * k, 4 * k + 4):
                    dve.tensor_tensor_scan(lh[:, t, :], la[:, t % 4, :], li[:, t % 4, :], 0.0, ALU.mult,
                                           ALU.add).then_inc(s_hl, 1)

            def gate_scaled(k):
                if k >= 2:
                    dve.wait_ge(s_ysum, 1)
                scaled(14 + k, gate_of(k))

            def lru_out(k):
                dve.wait_ge(s_gl, k + 1)
                dve.wait_ge(s_hl, 2 * k + 2)
                v = gate_of(k)
                dve.tensor_tensor(v, v, lh[:, 2 * k:2 * k + 2, :], ALU.mult).then_inc(s_yb, 1)

            def lru_lo(k):
                dve.wait_ge(s_yb, k + 1)
                for m in range(2):
                    dve.wait_ge(s_bhi, 2 * k + m + 1)
                    t = 8 + 2 * k + m
                    dve.tensor_tensor(hid[:, t, 1, :], gate_of(k)[:, m, :], hid[:, t, 0, :].bitcast(F32),
                                      ALU.subtract).then_inc(s_blo, 1)

            def y_rrms(g):
                dve.wait_ge(s_yrms, g + 1)
                dve.reciprocal(yrb[:, g, :], yrms[:, g, :]).then_inc(s_yrb, 1)

            def y_norm(g):
                dve.wait_ge(s_ybc, g + 1)
                dve.wait_ge(s_yg, 2 * g + 2)
                for t in range(4 * g, 4 * g + 4):
                    dve.scalar_tensor_tensor(xbc[:, t, :], xbc[:, t, :], column("ssd_norm", t), banks[2][:, 0:T],
                                             ALU.mult, ALU.mult).then_inc(s_yn, 1)

            def y_lo(t):
                dve.wait_ge(s_yn, t + 1)
                dve.wait_ge(s_yhi, t + 1)
                dve.tensor_tensor(hid[:, t, 1, :], xbc[:, t, :], hid[:, t, 0, :].bitcast(F32),
                                  ALU.subtract).then_inc(s_ylo, 1)

            todo = {s: [] for s in range(20)}
            todo[0] += [dt_weights]
            todo[2] += [softplus_args]
            todo[3] += [softplus_u]
            todo[4] += [lambda: softplus_ratio(U_, D_, M_)]
            todo[5] += [steps_of_dt]
            todo[6] += [sums_of_dt]
            todo[7] += [lambda: take_cb(0), lambda: take_cb(1)]
            todo[8] += [take_tok]
            for g, s in enumerate((8, 9, 9, 10)):
                todo[s] += [lambda g=g: take_x(g)]
            for m in range(8):
                todo[10 + m] += [lambda m=m: take_y(m)]
                todo[8 + m] += [lambda m=m: exponents(2 * m), lambda m=m: exponents(2 * m + 1)]
            todo[13] += [lambda: lru_mult2(0)]
            todo[15] += [lambda: lru_scan(0)]
            todo[17] += [lambda: lru_mult2(1), lambda: lru_out(0), lambda: y_rrms(0)]
            todo[18] += [lambda: y_norm(0), lambda: y_rrms(1), lambda: lru_scan(1), lambda: lru_out(1)]
            todo[18] += [lambda: lru_lo(0)] + [lambda t=t: y_lo(t) for t in range(4)]
            todo[19] += [lambda t=t: y_lo(t) for t in range(4, 8)] + [lambda: lru_lo(1)]
            for j in range(10):
                todo[j + 2] += [lambda j=j: conv_taps(j)]
            todo[7] += [scale_of_lambda]

            def read_pair(j):
                if j < 10:
                    scaled(j, pad[:, j % 2, :, 3:3 + T])
                elif j < 14:
                    scaled(j, sz[:, 2 * (j - 10):2 * (j - 10) + 2, :])
                else:
                    gate_scaled(j - 14)

            for s in range(20):
                if s < 2:
                    before[s]()
                if s >= 2:
                    read_pair(s - 2)
                if s == 19:
                    y_norm(1)
                convert_lo(dve, p0 + s, DT, s in ROUNDED_BY_VECTOR)
                if s == 1:
                    token_scale(dve, n)
                for task in todo[s]:
                    task()
            for k in (2, 3):
                lru_out(k)
            for k in (2, 3):
                lru_lo(k)

            def out_tile(d):
                p = p0 + 18 + d
                dve.wait_ge(s_blk, 2 * (p0 + 18) + OUT_BLOCKS.index((d, 1)) + 1)
                add_residual(dve, n, d, half(p, 0), 1.0)

            for s in range(20, 26):
                out_tile(s - 20)
                convert_lo(dve, p0 + s, DT)
            return [lambda: out_tile(DT - 2), lambda: out_tile(DT - 1)]

        def lxb(k):
            return xbc[:, 8:12, :] if k == 0 else lx_hi[:, :, :]

        def hyb_gpsimd(pool, n):
            def head_m(hd):
                pool.wait_ge(s_dec, hd + 1)
                if hd == 0:
                    pool.wait_ge(s_cb, 2)
                pool.tensor_tensor(seg_of(hd), seg_of(hd), cbm[:, hd // 8, :], ALU.mult).then_inc(s_m, 1)

            def lru_ix(k):
                pool.wait_ge(s_gs, 8 * k + 8)
                pool.tensor_tensor(li[:, :, :], li[:, :, :], lxb(k), ALU.mult).then_inc(s_ix, 1)

            def gate_y(k):
                pool.wait_ge(s_sz, k // 2 + 1)
                pool.wait_ge(s_yr, 2 * k + 2)
                y, z = xbc[:, 2 * k:2 * k + 2, :], sz[:, 2 * k:2 * k + 2, :]
                pool.tensor_tensor(y, y, z, ALU.mult).then_inc(s_yg, 1)
                pool.wait_ge(s_yg, k + 1)
                pool.tensor_tensor(z, y, y, ALU.mult).then_inc(s_ysq, 1)

            for m in range(8):
                head_m(2 * m)
                head_m(2 * m + 1)
                if m == 3:
                    lru_ix(0)
                if m in (5, 6):
                    gate_y(m - 5)
            gate_y(2)
            lru_ix(1)
            gate_y(3)

        s_lamin = sem("s_lamin")
        s_lam = sem("s_lam")
        s_lamp = sem("s_lamp")
        s_lame = sem("s_lame")
        s_mask = sem("s_mask")
        s_qkv = sem("s_qkv")
        s_rot = sem("s_rot")
        s_t1 = sem("s_t1")
        s_t2 = sem("s_t2")
        s_qr = sem("s_qr")
        s_sc = sem("s_sc")
        s_mx = sem("s_mx")
        s_nm = sem("s_nm")
        s_exp = sem("s_exp")
        s_at1 = sem("s_at1")
        s_tr = sem("s_tr")
        s_ats = sem("s_ats")
        s_vtp = sem("s_vtp")
        s_vt = sem("s_vt")
        s_o = sem("s_o")
        s_osq = sem("s_osq")
        s_orms = sem("s_orms")
        s_orb = sem("s_orb")
        s_on = sem("s_on")
        s_ot = sem("s_ot")
        s_ohi = sem("s_ohi")
        s_olo = sem("s_olo")

        W3 = 3 * P
        places, at = {}, 0
        for name, size in (("qk", 4 * T), ("t1", 2 * T), ("t2", 2 * T), ("qr", 4 * T), ("pr", 4 * W3), ("aa", 2 * W3),
                           ("tmp", W3), ("ats", AH * W3), ("vf", 4 * T), ("vt", TC * D), ("on", 4 * T), ("squares", 4 * T)):
            places[name] = arena[:, at:at + size]
            at += size
        qk = places["qk"].rearrange("p (b g t) -> p b g t", b=2, g=2)
        t1, t2 = (places[x].rearrange("p (g t) -> p g t", g=2) for x in ("t1", "t2"))
        qr = places["qr"].rearrange("p (b g t) -> p b g t", b=2, g=2)
        pr = places["pr"].rearrange("p (b c k) -> p b c k", b=2, c=2)
        aa = places["aa"].rearrange("p (b k) -> p b k", b=2)
        tmp = places["tmp"]
        ats = places["ats"].rearrange("p (h k) -> p h k", h=AH)
        vf = places["vf"].rearrange("p (b k) -> p b k", b=2)
        vt = places["vt"].rearrange("p (c e) -> p c e", c=TC)
        on, squares = (places[x].rearrange("p (b k e) -> p b k e", b=2, k=4) for x in ("on", "squares"))
        oss, orms, orb = (small[:, 42 + 8 * k:50 + 8 * k].rearrange("p (b k) -> p b k", b=2) for k in range(3))
        O_BANK, OT_BANK = (2, 2, 2, 5), (3, 3, 3, 6)
        maskb = arena[:, 14976:15104].bitcast(BF16)
        mx, nm, sm, rc = (small[:, 8 * k:8 * k + 8].rearrange("p (b k) -> p b k", b=2) for k in range(4))
        rl = small[:, 32:36].rearrange("p (b k) -> p b k", b=2)
        lam, wsub, lprod, lexp = small[:, 36:37], small[:, 37:38], small[0:64, 38:40], small[:, 40:42]
        lamin = small[0:64, 146:150]
        QB = [(0, P), (P, W3)]

        def out_acc(n, k):
            if k < 4:
                return (half(first[n] + 12, 0), half(first[n] + 13, 0), banks[4][:, 0:T], banks[7][:, 0:T])[k]
            return half(first[n] + 12 + k // 2, k % 2)

        def v_pair(i):
            return i if i < 2 else AH + i

        def att_sync(sp, n, i):
            b = 2 * first[n]
            w, wo = a["dif_w_qkv"][0], a["dif_w_o"][0]
            cols = [c for t in range(AH) for c in (P * t, D + P * t)]
            cols = [2 * D + P * t for t in range(4)] + cols + [2 * D + P * t for t in range(4, AH)]
            for c in cols:
                load(sp, b, b % RING, w[:, c:c + P].rearrange("(k p) m -> p k m", p=P), DT)
                b += 1
            for d in range(DT):
                load(sp, b, b % RING, wo[:, d * P:(d + 1) * P].rearrange("(k p) m -> p k m", p=P), DT)
                b += 1

        def att_tensor(pe, n, i):
            p0 = first[n]

            def lambda_sums():
                pe.wait_ge(s_lam, 1)
                pe.matmul(banks[3][:, 0:2], ones[0:64, :], lprod, start=True, stop=True).then_inc(s_lamp, 1)

            def turn(t):
                pe.wait_ge(s_qkv, t + 3)
                if t:
                    pe.wait_ge(s_t2, t)
                pe.matmul(banks[4][:, :], cst("rot"), qk[:, t % 2, :, :].rearrange("p g t -> p (g t)"), start=True,
                          stop=True).then_inc(s_rot, 1)

            def scores(t):
                pe.wait_ge(s_qr, t + 1)
                if t == 0:
                    pe.wait_ge(s_mask, 2)
                else:
                    pe.wait_ge(s_exp, 4 * t)
                for c in range(2):
                    o = banks[5 + c]
                    q, k = (qr[64 * c:64 * c + 64, t % 2, g, :] for g in range(2))
                    pe.matmul(o[:, P:T], q[:, P:T], k[:, 0:P], start=True, stop=True)
                    for qb, at_ in ((0, 0), (1, T)):
                        pe.matmul(o[:, at_:at_ + P], maskb[:, 0:P], maskb[:, P:2 * P], start=True, stop=False)
                        mm = pe.matmul(o[:, at_:at_ + P], q[:, qb * P:qb * P + P], k[:, qb * P:qb * P + P],
                                       start=False, stop=True)
                mm.then_inc(s_sc, 1)

            def weights_turned(t):
                pe.wait_ge(s_at1, 6 * t + 6)
                if t:
                    pe.wait_ge(s_ats, t)
                for k in range(3):
                    mm = pe.transpose(banks[7][:, k * P:k * P + P], aa[:, t % 2, k * P:k * P + P], ident)
                mm.then_inc(s_tr, 1)

            def v_turned(i):
                pe.wait_ge(s_qkv, v_pair(i) + 1)
                if i == 0:
                    pe.wait_ge(s_lame, 1)
                elif i == 2:
                    pe.wait_ge(s_t2, AH)
                else:
                    pe.wait_ge(s_vt, i)
                for c in range(TC):
                    for m in range(2):
                        mm = pe.transpose(banks[3 + i // 2][:, (2 * c + m) * P:(2 * c + m + 1) * P],
                                          vf[:, i % 2, m * T + c * P:m * T + c * P + P], ident)
                mm.then_inc(s_vtp, 1)

            def outputs(i):
                pe.wait_ge(s_vt, i + 1)
                pe.wait_ge(s_ats, 2 * i + 2)
                if i == 0:
                    pe.wait_ge(s_rms, n + 1)
                elif i < 3:
                    pe.wait_ge(s_on, i)
                else:
                    pe.wait_ge(s_exp, 4 * AH)
                for m in range(2):
                    t = 2 * i + m
                    o = banks[O_BANK[i]][:, m * T:(m + 1) * T]
                    v0, v1 = (vt[:, c, t * P:t * P + P] for c in range(TC))
                    pe.matmul(o[:, 0:P], ats[:, t, 0:P], v0, start=True, stop=True)
                    pe.matmul(o[:, P:T], ats[:, t, P:T], v0, start=True, stop=False)
                    mm = pe.matmul(o[:, P:T], ats[:, t, T:W3], v1, start=False, stop=True)
                mm.then_inc(s_o, 1)

            def outputs_turned(i):
                pe.wait_ge(s_on, i + 1)
                if i == 0:
                    pe.wait_ge(s_vt, 2)
                elif i < 3:
                    pe.wait_ge(s_olo, i)
                for k in range(4):
                    mm = pe.transpose(banks[OT_BANK[i]][:, k * P:(k + 1) * P], on[:, i % 2, k, :], ident)
                mm.then_inc(s_ot, 1)

            after = {s: [] for s in range(12)}
            after[0] += [lambda_sums]
            for t in range(AH):
                if t < 6:
                    after[t + 6] += [lambda t=t: weights_turned(t)]
            for t in range(AH):
                after[t + 4] += [lambda t=t: scores(t)]
            for t in range(AH):
                after[t + 3] += [lambda t=t: turn(t)]
            after[1] += [lambda: v_turned(0)]
            after[2] += [lambda: v_turned(1)]
            after[8] += [lambda: outputs(0)]
            after[10] += [lambda: outputs(1), lambda: outputs_turned(0)]
            after[11] += [lambda: v_turned(2), lambda: outputs_turned(1)]
            for j in range(12):
                read_out(pe, p0 + j - 2)
                for m in range(2):
                    b = 2 * (p0 + j) + m
                    multiply(pe, b, b % RING, DT, xn, 0, half(p0 + j, m),
                             need=(lambda t: pe.wait_ge(s_xlo, DT * n + t + 1)) if j + m == 0 else None)
                if j == 0:
                    token_sums(pe, n)
                for task in after[j]:
                    task()

            def out_block(k, part=None):
                b = 2 * (p0 + 12) + k
                if part is None or part[0] == 0:
                    if k == 2:
                        pe.wait_ge(s_vt, 4)
                    elif k != 3:
                        read_out(pe, p0 + (10, 11, 0, 0, 12, 12, 13, 13)[k])
                multiply(pe, b, b % RING, DT, hid, 0, out_acc(n, k),
                         need=(lambda t: pe.wait_ge(s_olo, t // 2 + 1)) if k == 0 else None, part=part)

            out_block(0, range(0, 4))
            v_turned(3)
            out_block(1, range(0, 4))
            weights_turned(6)
            outputs(2)
            out_block(2, range(0, 4))
            weights_turned(7)
            outputs_turned(2)
            outputs(3)
            for k in range(3):
                out_block(k, range(4, 6))
            outputs_turned(3)
            for k in range(3):
                out_block(k, range(6, 8))
            for k in range(3, DT):
                out_block(k)

        def att_scalar(act, n, i, before):
            p0 = first[n]

            def lambda_exp():
                act.wait_ge(s_lamp, 1)
                act.activation(lexp, banks[3][:, 0:2], ACT.Exp).then_inc(s_lame, 1)

            def exponentials(t):
                act.wait_ge(s_nm, t + 1)
                for qb, (lo, hi) in enumerate(QB):
                    for c in range(2):
                        k = 2 * qb + c
                        act.activation(pr[:, t % 2, c, lo:hi], banks[5 + c][:, lo:hi], ACT.Exp, scale=0.125,
                                       bias=nm[:, t % 2, k:k + 1], accum_out=sm[:, t % 2, k:k + 1]).then_inc(s_exp, 1)

            def take_weights(t):
                act.wait_ge(s_tr, t + 1)
                act.activation(ats[:, t, :], banks[7][:, 0:W3], ACT.Copy).then_inc(s_ats, 1)

            def take_v(i):
                act.wait_ge(s_vtp, i + 1)
                act.activation(vt[:, :, i * T:(i + 1) * T], banks[3 + i // 2][:, :].rearrange("p (c e) -> p c e", c=TC),
                               ACT.Copy).then_inc(s_vt, 1)

            def output_rms(i):
                act.wait_ge(s_o, i + 1)
                if i >= 2:
                    act.wait_ge(s_orb, i - 1)
                for k in range(4):
                    act.activation(squares[:, i % 2, k, :], banks[O_BANK[i]][:, k * P:(k + 1) * P], ACT.Square,
                                   accum_out=oss[:, i % 2, k:k + 1]).then_inc(s_osq, 1)
                act.wait_ge(s_osq, 4 * i + 4)
                act.activation(orms[:, i % 2, :], oss[:, i % 2, :], ACT.Sqrt, scale=1.0 / P,
                               bias=eps[:, 0:1]).then_inc(s_orms, 1)

            def output_hi(i):
                act.wait_ge(s_ot, i + 1)
                act.activation(hid[:, 2 * i:2 * i + 2, 0, :], banks[OT_BANK[i]][:, :].rearrange("p (m t) -> p m t", m=2),
                               ACT.Copy, scale=wsub).then_inc(s_ohi, 1)

            todo = {s: [] for s in range(14)}
            todo[2] += [lambda_exp]
            todo[3] += [lambda: take_v(0)]
            todo[4] += [lambda: take_v(1)]
            todo[13] += [lambda: take_v(2)]
            for t in range(6):
                todo[t + 8] += [lambda t=t: take_weights(t)]
            todo[13] += [lambda: output_hi(1)]
            for t in range(AH):
                todo[t + 6] += [lambda t=t: exponentials(t)]
            todo[10] += [lambda: output_rms(0)]
            todo[12] += [lambda: output_hi(0), lambda: output_rms(1)]
            for s in range(14):
                if s < 2:
                    before[s]()
                convert_hi(act, p0 + s, DT)
                if s == 1:
                    token_rms(act, n)
                for task in todo[s]:
                    task()
            take_weights(6)
            take_v(3)
            output_rms(2)
            output_hi(2)
            take_weights(7)
            output_rms(3)
            output_hi(3)
            for s in (14, 15):
                for m in range(2):
                    residual_hi(act, n + 1, 2 * (s - 14) + m)
                convert_hi(act, p0 + s, DT)
            return [lambda: [residual_hi(act, n + 1, d) for d in (4, 5)],
                    lambda: [residual_hi(act, n + 1, d) for d in (6, 7)]]

        def att_vector(dve, n, i, before):
            p0 = first[n]

            def lambda_products():
                dve.wait_ge(s_lamin, 16)
                dve.tensor_tensor(lprod, lamin[:, 0:2], lamin[:, 2:4], ALU.mult).then_inc(s_lam, 1)
                dve.tensor_copy(maskb[:, 0:P], ident).then_inc(s_mask, 1)
                dve.tensor_copy(maskb[:, P:2 * P], cst("neg")).then_inc(s_mask, 1)

            def lambda_value():
                dve.wait_ge(s_lame, 1)
                dve.tensor_tensor(lam, lexp[:, 0:1], lexp[:, 1:2], ALU.subtract).then_inc(s_lam, 1)
                dve.wait_ge(s_lam, 2)
                dve.tensor_scalar(lam, lam, LAMBDA_INIT, None, ALU.add).then_inc(s_lam, 1)
                dve.tensor_scalar(wsub, vec[:, VEC["dif_subln"]:VEC["dif_subln"] + 1], 1.0 - LAMBDA_INIT, None,
                                  ALU.mult).then_inc(s_lam, 1)
                dve.wait_ge(s_lam, 4)

            def scaled(j, dst):
                dve.wait_ge(s_blk, 2 * (p0 + j) + 2)
                dve.tensor_tensor(dst, both(p0 + j), rb2, ALU.mult).then_inc(s_qkv, 1)

            def qk_scaled(t):
                if t >= 2:
                    dve.wait_ge(s_t1, t - 1)
                    dve.wait_ge(s_rot, t - 1)
                scaled(t + 2, qk[:, t % 2, :, :])

            def rope(t):
                dve.wait_ge(s_rot, t + 1)
                dve.tensor_tensor(t2, banks[4][:, :].rearrange("p (g t) -> p g t", g=2),
                                  cst("sin").unsqueeze(1).to_broadcast([P, 2, T]), ALU.mult).then_inc(s_t2, 1)
                dve.wait_ge(s_t2, t + 1)
                dve.wait_ge(s_t1, t + 1)
                if t >= 2:
                    dve.wait_ge(s_sc, t - 1)
                dve.tensor_tensor(qr[:, t % 2, :, :], t1, t2, ALU.add).then_inc(s_qr, 1)

            def maxima(t):
                dve.wait_ge(s_sc, t + 1)
                for qb, (lo, hi) in enumerate(QB):
                    dve.tensor_reduce(mx[:, t % 2, 2 * qb:2 * qb + 2], scores_ps[:, :, lo:hi], AX,
                                      ALU.max).then_inc(s_mx, 1)
                dve.wait_ge(s_mx, 2 * t + 2)
                dve.tensor_scalar(nm[:, t % 2, :], mx[:, t % 2, :], -0.125, None, ALU.mult).then_inc(s_nm, 1)

            def head_weights(t):
                c = [6 * t]

                def link(ins):
                    ins.then_inc(s_at1, 1)
                    c[0] += 1
                    dve.wait_ge(s_at1, c[0])

                b = t % 2
                dve.wait_ge(s_exp, 4 * t + 4)
                link(dve.reciprocal(rc[:, b, :], sm[:, b, :]))
                link(dve.tensor_scalar(rl[:, b, :], rc[:, b, 1:4:2], lam, None, ALU.mult))
                if t >= 2:
                    dve.wait_ge(s_tr, t - 1)
                for qb, (lo, hi) in enumerate(QB):
                    link(dve.tensor_scalar(tmp[:, lo:hi], pr[:, b, 1, lo:hi], rl[:, b, qb:qb + 1], None, ALU.mult))
                    link(dve.scalar_tensor_tensor(aa[:, b, lo:hi], pr[:, b, 0, lo:hi], rc[:, b, 2 * qb:2 * qb + 1],
                                                  tmp[:, lo:hi], ALU.mult, ALU.subtract))

            def v_scaled(i):
                if i >= 2:
                    dve.wait_ge(s_vtp, i - 1)
                scaled(v_pair(i), vf[:, i % 2, :].rearrange("p (g t) -> p g t", g=2))

            def output_norm(i):
                dve.wait_ge(s_orms, i + 1)
                dve.reciprocal(orb[:, i % 2, :], orms[:, i % 2, :]).then_inc(s_orb, 1)
                dve.wait_ge(s_orb, i + 1)
                if i >= 2:
                    dve.wait_ge(s_ot, i - 1)
                dve.tensor_tensor(on[:, i % 2, :, :], banks[O_BANK[i]][:, :].rearrange("p (k e) -> p k e", k=4),
                                  orb[:, i % 2, :].unsqueeze(2).to_broadcast([P, 4, P]), ALU.mult).then_inc(s_on, 1)

            def output_lo(i):
                dve.wait_ge(s_ohi, i + 1)
                dve.scalar_tensor_tensor(hid[:, 2 * i:2 * i + 2, 1, :],
                                         banks[OT_BANK[i]][:, :].rearrange("p (m t) -> p m t", m=2), wsub,
                                         hid[:, 2 * i:2 * i + 2, 0, :].bitcast(F32), ALU.mult,
                                         ALU.subtract).then_inc(s_olo, 1)

            def read_pair(j):
                if 2 <= j < 2 + AH:
                    qk_scaled(j - 2)
                else:
                    v_scaled(j if j < 2 else j - AH)

            todo = {s: [] for s in range(14)}
            todo[0] += [lambda_products]
            todo[2] += [lambda_value]
            for t in range(AH):
                todo[t + 6] += [lambda t=t: maxima(t)]
            for t in range(AH):
                todo[t + 5] += [lambda t=t: rope(t)]
            todo[13] += [lambda: output_lo(1)]
            for t in range(AH):
                todo[t + 6] += [lambda t=t: head_weights(t)]
            todo[10] += [lambda: output_norm(0)]
            todo[12] += [lambda: output_lo(0), lambda: output_norm(1)]
            for s in range(14):
                if s < 2:
                    before[s]()
                if s >= 2:
                    read_pair(s - 2)
                convert_lo(dve, p0 + s, DT)
                if s == 1:
                    token_scale(dve, n)
                for task in todo[s]:
                    task()
            output_norm(2)
            output_lo(2)
            output_norm(3)
            output_lo(3)

            def out_pair(e):
                p = p0 + 12 + e
                dve.wait_ge(s_blk, 2 * p + 2)
                for m in range(2):
                    add_residual(dve, n, 2 * e + m, out_acc(n, 2 * e + m), 1.0)

            for s in (14, 15):
                out_pair(s - 14)
                convert_lo(dve, p0 + s, DT)
            return [lambda: out_pair(2), lambda: out_pair(3)]

        def att_gpsimd(pool, n):
            for t in range(AH):
                pool.wait_ge(s_qkv, t + 3)
                if t:
                    pool.wait_ge(s_qr, t)
                pool.tensor_tensor(t1, qk[:, t % 2, :, :], cst("cos").unsqueeze(1).to_broadcast([P, 2, T]),
                                   ALU.mult).then_inc(s_t1, 1)

        fin = arena[:, 4096:4096 + DT * T].rearrange("p (d t) -> p d t", d=DT)
        last = len(phases)
        block = ctx.enter_context(nc.Block())

        @block.sync
        def _(sp):
            sp.dma_start(vec[:], a["vec"]).then_inc(s_const, 16)
            sp.dma_start(h[:], a["xT"].rearrange("(d p) t -> p d t", p=P)).then_inc(s_x, 16)
            sp.dma_start(con[:], a["con"]).then_inc(s_const, 16)
            sp.dma_start(heads[:], a["heads"]).then_inc(s_const, 16)
            for n, (kind, i) in enumerate(phases):
                {"ffn": ffn_sync, "hyb": hyb_sync, "att": att_sync}[kind](sp, n, i)
            sp.wait_ge(s_fin, DT)
            sp.dma_start(out.rearrange("(d p) t -> p d t", p=P), fin).then_inc(s_out, 16)
            sp.wait_ge(s_out, 16)

        @block.tensor
        def _(pe):
            pe.wait_ge(s_const, 48)
            for n, (kind, i) in enumerate(phases):
                {"ffn": ffn_tensor, "hyb": hyb_tensor, "att": att_tensor}[kind](pe, n, i)
            token_sums(pe, last)

        @block.scalar
        def _(act):
            act.wait_ge(s_const, 48)
            act.wait_ge(s_eps, 1)
            for d in range(DT):
                residual_hi(act, 0, d)
            before = [lambda: None] * 2
            for n, (kind, i) in enumerate(phases):
                before = {"ffn": ffn_scalar, "hyb": hyb_scalar, "att": att_scalar}[kind](act, n, i, before)
            token_rms(act, last)

        @block.vector
        def _(dve):
            dve.memset(eps[:], EPS).then_inc(s_eps, 1)
            dve.wait_ge(s_const, 48)
            for d in range(DT):
                residual_lo(dve, 0, d)
            before = [lambda: None] * 2
            for n, (kind, i) in enumerate(phases):
                before = {"ffn": ffn_vector, "hyb": hyb_vector, "att": att_vector}[kind](dve, n, i, before)
            for left in before:
                left()
            token_scale(dve, last)
            for d in range(DT):
                w = VEC["final_norm"] + d
                dve.scalar_tensor_tensor(fin[:, d, :], h[:, d, :], vec[:, w:w + 1], rb[:], ALU.mult,
                                         ALU.mult).then_inc(s_fin, 1)

        @block.gpsimd
        def _(pool):
            if any(kind == "hyb" for kind, _ in phases):
                hyb_weights(pool)
            pool.dma_start(lamin, a["lam"]).then_inc(s_lamin, 16)
            for n in range(len(phases) + 1):
                for d in range(DT):
                    residual_square(pool, n, d)
                if n < len(phases) and phases[n][0] != "ffn":
                    {"hyb": hyb_gpsimd, "att": att_gpsimd}[phases[n][0]](pool, n)


MATRICES = ["ffn1_gate", "ffn1_up", "ffn1_down", "ffn2_gate", "ffn2_up", "ffn2_down", "hyb_w_in", "hyb_w_out",
            "dif_w_qkv", "dif_w_o", "lru_w_ra", "lru_w_ix"]


def tables():
    con = np.zeros((P, NCON), np.float32)

    def put(name, v):
        con[:, CON[name][0]:CON[name][1]] = v

    put("ident", np.eye(P))
    put("ones", 1.0)
    put("tri", np.triu(np.ones((P, P))))
    put("neg", np.triu(np.full((P, P), MASKED), 1))
    hd, rot = 64, 16
    half = rot // 2
    inv = np.float32(500000.0) ** (-np.arange(0, rot, 2, dtype=np.float32) / np.float32(rot))
    ang = np.arange(T, dtype=np.float32)[:, None] * inv[None, :].astype(np.float32)
    cos, sin = np.ones((P, T), np.float32), np.zeros((P, T), np.float32)
    turn = np.zeros((P, P), np.float32)
    for c in range(P // hd):
        for r in range(half):
            lo, hi = c * hd + r, c * hd + half + r
            cos[lo] = cos[hi] = np.cos(ang[:, r])
            sin[lo] = sin[hi] = np.sin(ang[:, r])
            turn[hi, lo], turn[lo, hi] = -1.0, 1.0
    put("rot", turn)
    put("cos", cos)
    put("sin", sin)
    return con


def kernel(**inputs):
    import numpy as _np
    import concourse.bacc as _bacc
    from concourse import mybir as _mybir
    from concourse.bass_utils import run_bass_kernel_spmd as _run

    x = {k: _np.asarray(v) for k, v in inputs.items()}
    order = ("norm_ff1", "norm_mix", "norm_ff2", "final_norm", "ssd_conv_w", "ssd_conv_b", "lru_conv_w", "lru_conv_b",
             "lru_b_ra", "lru_b_ix", "lru_lambda", "ssd_norm")
    rows = [x[k].reshape(-1, P) for k in order]
    rows += [_np.repeat(x["ssd_d"].reshape(-1), HD).reshape(-1, P), x["dif_subln"].reshape(-1, P)]
    arrays = {
        "xT": _np.ascontiguousarray(x["x"][0].T),
        "vec": _np.ascontiguousarray(_np.concatenate(rows, axis=0).T),
        "heads": _np.ascontiguousarray(_np.stack([x[k][0] for k in ("ssd_dt_bias", "ssd_a_log", "ssd_d")], axis=1)),
        "lam": _np.ascontiguousarray(_np.stack([x[k][0] for k in ("dif_lq1", "dif_lq2", "dif_lk1", "dif_lk2")], axis=1)),
        "con": tables(),
    }
    for k in MATRICES:
        arrays[k] = _np.ascontiguousarray(x[k])
    nc = _bacc.Bacc("TRN2", target_bir_lowering=False, num_devices=1)
    args = {k: nc.dram_tensor(f"in_{k}", v.shape, _mybir.dt.from_np(v.dtype), kind="ExternalInput").ap()
            for k, v in arrays.items()}
    out = nc.dram_tensor("out_h", (D, T), _mybir.dt.float32, kind="ExternalOutput").ap()
    trunk(nc, args, out)
    r = _run(nc, [{f"in_{k}": v for k, v in arrays.items()}], core_ids=[0])
    return _np.ascontiguousarray(r.results[0]["out_h"].T)[None]
```
